# Optimizing a Trainium2 kernel written in Bass

```python
import jax, jax.numpy as jnp
from jax import lax
import numpy as np

D_MODEL = 1024
BATCH = 1
SEQ = 256
DEPTH = 2
DEC_BATCH = 8
DEC_SEQ = 1
PAST_LEN = 2048
PAGE_SIZE = 128

D_A = D_MODEL // 2
D_B = D_MODEL // 2
CONV_A = 3
CONV_B = 31
D_IN = 3 * D_A + 2 * D_B
POOL_WINDOWS = (2, 4, 8, 16)
N_POOL = len(POOL_WINDOWS)
POOL_GROUP = D_MODEL // N_POOL
POOL_CTX = max(POOL_WINDOWS) - 1
D_FF = 2816
N_EXPERTS = 8
TOP_K = 2
D_FF_EXPERT = 3584
MOE_BLOCK = 128
N_EVEN = (DEPTH + 1) // 2
N_ODD = DEPTH // 2
EPS = 1e-6

kernel_name = "hybrid_conv_pool_moe_adaln_step"

def rmsnorm(x, g):
    xf = x.astype(jnp.float32)
    y = xf * lax.rsqrt(jnp.mean(xf * xf, axis=-1, keepdims=True) + EPS)
    return (y * g.astype(jnp.float32)).astype(x.dtype)

def layernorm(x, g, b):
    xf = x.astype(jnp.float32)
    mu = jnp.mean(xf, axis=-1, keepdims=True)
    var = jnp.mean(jnp.square(xf - mu), axis=-1, keepdims=True)
    y = (xf - mu) * lax.rsqrt(var + EPS)
    return (y * g.astype(jnp.float32) + b.astype(jnp.float32)).astype(x.dtype)

def causal_depthwise_conv(u, buf, w):
    k = w.shape[0]
    upad = jnp.concatenate([buf.astype(u.dtype), u], axis=1)
    y = lax.conv_general_dilated(upad, w[:, None, :].astype(u.dtype), (1,), 'VALID',
                                 dimension_numbers=('NWC', 'WIO', 'NWC'),
                                 feature_group_count=u.shape[-1])
    return y, upad[:, upad.shape[1] - (k - 1):]

def conv_pair_mixer(h, buf_a, buf_b, w_in, w_conv_a, w_conv_b, b_conv_b, ln_g, ln_b, w_out):
    u = h @ w_in
    a_b, a_c, a_x, b_v, b_g = jnp.split(u, [D_A, 2 * D_A, 3 * D_A, 3 * D_A + D_B], axis=-1)
    ya, new_a = causal_depthwise_conv(a_c * a_x, buf_a, w_conv_a)
    ya = a_b * ya
    glu = b_v * jax.nn.sigmoid(b_g)
    yb, new_b = causal_depthwise_conv(glu, buf_b, w_conv_b)
    yb = jax.nn.silu(layernorm(yb + b_conv_b, ln_g, ln_b))
    y = jnp.concatenate([ya, yb], axis=-1) @ w_out
    return y, new_a, new_b

def pool_mixer(h, buf, start_pos, w_pool, scale):
    n, t, d = h.shape
    upad = jnp.concatenate([buf.astype(h.dtype), h], axis=1)
    cs = jnp.cumsum(upad.astype(jnp.float32), axis=1)
    cs = jnp.concatenate([jnp.zeros((n, 1, d), jnp.float32), cs], axis=1)
    pos = start_pos + jnp.arange(t)
    hf = h.astype(jnp.float32)
    off = POOL_CTX + 1
    groups = []
    for gi, win in enumerate(POOL_WINDOWS):
        sl = slice(gi * POOL_GROUP, (gi + 1) * POOL_GROUP)
        s = cs[:, off:off + t, sl] - cs[:, off - win:off - win + t, sl]
        cnt = jnp.minimum(pos + 1, win).astype(jnp.float32)[None, :, None]
        groups.append(s / cnt - hf[..., sl])
    diff = jnp.stack(groups, axis=2).astype(h.dtype)
    y = jnp.einsum('ntgc,gcd->ntgd', diff, w_pool).reshape(n, t, d)
    return y * scale, upad[:, upad.shape[1] - POOL_CTX:]

def swiglu(h, w_gate, w_up, w_down):
    return (jax.nn.silu(h @ w_gate) * (h @ w_up)) @ w_down

def moe_swiglu(h, w_router, b_router, w_gate, w_up, w_down):
    n, t, d = h.shape
    T = n * t
    xt = h.reshape(T, d)
    logits = xt.astype(jnp.float32) @ w_router.astype(jnp.float32) + b_router.astype(jnp.float32)
    probs = jax.nn.softmax(logits, axis=-1)
    top_p, top_e = lax.top_k(probs, TOP_K)
    top_p = top_p / jnp.sum(top_p, axis=-1, keepdims=True)
    flat_e = top_e.reshape(-1).astype(jnp.int32)
    flat_tok = jnp.repeat(jnp.arange(T, dtype=jnp.int32), TOP_K)
    flat_p = top_p.reshape(-1)
    order = jnp.argsort(flat_e, stable=True)
    se = flat_e[order]
    counts = jnp.zeros((N_EXPERTS,), jnp.int32).at[flat_e].add(1)
    padded = (counts + MOE_BLOCK - 1) // MOE_BLOCK * MOE_BLOCK
    pend = jnp.cumsum(padded)
    pstart = pend - padded
    ustart = jnp.cumsum(counts) - counts
    dest = pstart[se] + jnp.arange(T * TOP_K, dtype=jnp.int32) - ustart[se]
    n_blocks = -(-(T * TOP_K) // MOE_BLOCK) + N_EXPERTS
    n_slots = n_blocks * MOE_BLOCK
    slot_tok = jnp.full((n_slots,), T, jnp.int32).at[dest].set(flat_tok[order])
    slot_p = jnp.zeros((n_slots,), jnp.float32).at[dest].set(flat_p[order])
    block_e = jnp.minimum(jnp.searchsorted(pend, jnp.arange(n_blocks) * MOE_BLOCK, side='right'),
                          N_EXPERTS - 1).astype(jnp.int32)
    x_ext = jnp.concatenate([xt, jnp.zeros((1, d), xt.dtype)], axis=0)
    xs = x_ext[slot_tok].reshape(n_blocks, MOE_BLOCK, d)

    def expert_block(args):
        xb, e = args
        return swiglu(xb, w_gate[e], w_up[e], w_down[e])

    ys = lax.map(expert_block, (xs, block_e)).reshape(n_slots, d)
    out = jnp.zeros((T + 1, d), jnp.float32).at[slot_tok].add(ys.astype(jnp.float32) * slot_p[:, None])
    return out[:T].astype(h.dtype).reshape(n, t, d)

def _trunk(x, c, st_a, st_b, st_c, start_pos, p):
    new_a, new_b, new_c = [], [], []
    cs = jax.nn.silu(c)
    for i in range(DEPTH):
        j = i // 2
        mod = (cs @ p['w_ada'][i] + p['b_ada'][i])[:, None, :]
        sh_m, sc_m, g_m, sh_f, sc_f, g_f = jnp.split(mod, 6, axis=-1)
        h = rmsnorm(x, p['norm_mix'][i]) * (1 + sc_m) + sh_m
        if i % 2 == 0:
            y, na, nb = conv_pair_mixer(h, st_a[j], st_b[j], p['w_in'][j], p['w_conv_a'][j],
                                        p['w_conv_b'][j], p['b_conv_b'][j], p['ln_b_g'][j],
                                        p['ln_b_b'][j], p['w_out'][j])
            new_a.append(na)
            new_b.append(nb)
        else:
            y, nc = pool_mixer(h, st_c[j], start_pos, p['w_pool'][j], p['pool_scale'][j])
            new_c.append(nc)
        x = x + g_m * y
        h = rmsnorm(x, p['norm_ffn'][i]) * (1 + sc_f) + sh_f
        if i % 2 == 0:
            f = swiglu(h, p['w_ffn_gate'][j], p['w_ffn_up'][j], p['w_ffn_down'][j])
        else:
            f = moe_swiglu(h, p['w_router'][j], p['b_router'][j], p['w_exp_gate'][j],
                           p['w_exp_up'][j], p['w_exp_down'][j])
        x = x + g_f * f
    y = rmsnorm(x, p['norm_out'])
    return y, jnp.stack(new_a), jnp.stack(new_b), jnp.stack(new_c)

def setup_inputs(seed: int = 0) -> dict:
    key = jax.random.key(seed)
    ks = jax.random.split(key, 32)
    f32 = jnp.float32
    nrm = lambda k, s, sc: jax.random.normal(k, s, f32) * sc
    D = D_MODEL
    return {
        "x_prompt": nrm(ks[0], (BATCH, SEQ, D), 1.0),
        "x_sample": nrm(ks[1], (DEC_BATCH, DEC_SEQ, D), 1.0),
        "state_a": nrm(ks[2], (N_EVEN, DEC_BATCH, CONV_A - 1, D_A), 1.0),
        "state_b": nrm(ks[3], (N_EVEN, DEC_BATCH, CONV_B - 1, D_B), 0.5),
        "state_c": nrm(ks[4], (N_ODD, DEC_BATCH, POOL_CTX, D), 1.0),
        "c_prompt": nrm(ks[5], (BATCH, D), 1.0),
        "c_sample": nrm(ks[6], (DEC_BATCH, D), 1.0),
        "w_ada": nrm(ks[7], (DEPTH, D, 6 * D), 0.5 * D ** -0.5),
        "b_ada": nrm(ks[8], (DEPTH, 6 * D), 0.02),
        "norm_mix": 1.0 + nrm(ks[9], (DEPTH, D), 0.02),
        "norm_ffn": 1.0 + nrm(ks[10], (DEPTH, D), 0.02),
        "norm_out": 1.0 + nrm(ks[11], (D,), 0.02),
        "w_in": nrm(ks[12], (N_EVEN, D, D_IN), D ** -0.5),
        "w_conv_a": nrm(ks[13], (N_EVEN, CONV_A, D_A), CONV_A ** -0.5),
        "w_conv_b": nrm(ks[14], (N_EVEN, CONV_B, D_B), CONV_B ** -0.5),
        "b_conv_b": nrm(ks[15], (N_EVEN, D_B), 0.02),
        "ln_b_g": 1.0 + nrm(ks[16], (N_EVEN, D_B), 0.02),
        "ln_b_b": nrm(ks[17], (N_EVEN, D_B), 0.02),
        "w_out": nrm(ks[18], (N_EVEN, D_A + D_B, D), (D_A + D_B) ** -0.5),
        "w_ffn_gate": nrm(ks[19], (N_EVEN, D, D_FF), D ** -0.5),
        "w_ffn_up": nrm(ks[20], (N_EVEN, D, D_FF), D ** -0.5),
        "w_ffn_down": nrm(ks[21], (N_EVEN, D_FF, D), D_FF ** -0.5),
        "w_pool": nrm(ks[22], (N_ODD, N_POOL, POOL_GROUP, POOL_GROUP), POOL_GROUP ** -0.5),
        "pool_scale": 1.0 + nrm(ks[23], (N_ODD, D), 0.1),
        "w_router": nrm(ks[24], (N_ODD, D, N_EXPERTS), D ** -0.5),
        "b_router": nrm(ks[25], (N_ODD, N_EXPERTS), 0.01),
        "w_exp_gate": nrm(ks[26], (N_ODD, N_EXPERTS, D, D_FF_EXPERT), D ** -0.5),
        "w_exp_up": nrm(ks[27], (N_ODD, N_EXPERTS, D, D_FF_EXPERT), D ** -0.5),
        "w_exp_down": nrm(ks[28], (N_ODD, N_EXPERTS, D_FF_EXPERT, D), D_FF_EXPERT ** -0.5),
    }

def reference(x_prompt, x_sample, state_a, state_b, state_c, c_prompt, c_sample,
              w_ada, b_ada, norm_mix, norm_ffn, norm_out, w_in, w_conv_a, w_conv_b, b_conv_b,
              ln_b_g, ln_b_b, w_out, w_ffn_gate, w_ffn_up, w_ffn_down, w_pool, pool_scale,
              w_router, b_router, w_exp_gate, w_exp_up, w_exp_down):
    p = {
        'w_ada': w_ada, 'b_ada': b_ada, 'norm_mix': norm_mix, 'norm_ffn': norm_ffn,
        'norm_out': norm_out, 'w_in': w_in, 'w_conv_a': w_conv_a, 'w_conv_b': w_conv_b,
        'b_conv_b': b_conv_b, 'ln_b_g': ln_b_g, 'ln_b_b': ln_b_b, 'w_out': w_out,
        'w_ffn_gate': w_ffn_gate, 'w_ffn_up': w_ffn_up, 'w_ffn_down': w_ffn_down,
        'w_pool': w_pool, 'pool_scale': pool_scale, 'w_router': w_router, 'b_router': b_router,
        'w_exp_gate': w_exp_gate, 'w_exp_up': w_exp_up, 'w_exp_down': w_exp_down,
    }
    nb = x_prompt.shape[0]
    dt = x_prompt.dtype
    z_a = jnp.zeros((N_EVEN, nb, CONV_A - 1, D_A), dt)
    z_b = jnp.zeros((N_EVEN, nb, CONV_B - 1, D_B), dt)
    z_c = jnp.zeros((N_ODD, nb, POOL_CTX, D_MODEL), dt)
    y_prompt, pa, pb, pc = _trunk(x_prompt, c_prompt, z_a, z_b, z_c, 0, p)
    y_sample, sa, sb, sc = _trunk(x_sample, c_sample, state_a, state_b, state_c, PAST_LEN, p)
    return (y_prompt, y_sample, pa, sa, pb, sb, pc, sc)


_drawn_inputs = setup_inputs


def setup_inputs(seed=0):
    import zlib

    import numpy as np

    out = dict(_drawn_inputs(seed))
    spreads = {}
    factors = {'norm_out': 22.027,
     'b_conv_b': 8.0,
     'ln_b_g': 24.739,
     'ln_b_b': 27.187,
     'norm_ffn': 5.357,
     'pool_scale': 9.843,
     'b_router': 8.0}
    for name, (base, spread) in spreads.items():
        noise = np.random.default_rng([zlib.crc32(name.encode()), seed]).standard_normal(out[name].shape)
        drawn = base * np.exp(spread * noise) if base else spread * noise
        out[name] = __import__('jax').numpy.asarray(drawn.astype(out[name].dtype))
    for name, factor in factors.items():
        out[name] = (out[name] * factor).astype(out[name].dtype)
    return out
```

```python
from contextlib import ExitStack

import concourse.bass as bass
from concourse import mybir

F32 = mybir.dt.float32
I32 = mybir.dt.int32
ALU = mybir.AluOpType
ACT = mybir.ActivationFunctionType
AX_X = mybir.AxisListType.X

P = 128
D = 1024
DT = D // P
NP = 256
NS = 8
NT = NP + NS
NC = 1 + NS
DA = 512
CT = DA // P
KA, KB = 3, 31
WINDOWS = (2, 4, 8, 16)
CTX = max(WINDOWS) - 1
DFF = 2816
FT = DFF // P
NE = 8
DFE = 3584
EPS = 1e-6

UNIT = 2048
RING = 14
BLK = 512
KH = 2
NARROW, WIDE = 96, 160
PAIRS = DFE // (2 * P)
CHUNKS = DFE // BLK
EXPERT_UNITS = CHUNKS * 2 * KH + PAIRS
TILES = ((0, P), (P, P), (NP, NS))


IN_ORDER = (4, 3, 1, 2, 0)
FFN_STEPS = -(-DFF // BLK)
HALF_BLOCKS = 3 * D // BLK


def schedule():
    steps = [("ada", 0, b) for b in range(HALF_BLOCKS)]
    b = HALF_BLOCKS
    for i, blk in enumerate(IN_ORDER):
        steps.append(("in", blk))
        for _ in range(2 if i == len(IN_ORDER) - 1 else 1):
            steps.append(("ada", 0, b))
            b += 1
    steps += [("mid",), ("out", 0), ("out", 1), ("norm1",)]
    for i in range(FFN_STEPS):
        steps += [("gate", i), ("up", i), ("ada", 1, 2 * i), ("ada", 1, 2 * i + 1)]
    steps += [("state_c",), ("down", 0), ("down", 1)]
    return steps


def ffn_tiles(i):
    return range(4 * i, min(4 * i + 4, FT))


def weight_stream(w_ada, w_in, w_out, w_gate, w_up, w_down, w_pool):
    units = []

    def block(w, c0, cols=BLK):
        rows = w.shape[0] // P
        for k0 in range(0, rows, 4):
            kn = min(4, rows - k0)
            units.append((w[k0 * P:(k0 + kn) * P, c0:c0 + cols].rearrange("(k p) n -> p k n", p=P), kn, cols))

    for step in schedule():
        if step[0] == "ada":
            block(w_ada[step[1]], step[2] * BLK)
        elif step[0] in ("in", "out", "down"):
            block({"in": w_in, "out": w_out, "down": w_down}[step[0]][0], step[1] * BLK)
        elif step[0] in ("gate", "up"):
            c0 = step[1] * BLK
            block((w_gate if step[0] == "gate" else w_up)[0], c0, min(BLK, DFF - c0))
    units.append((w_pool[0].rearrange("g (k p) n -> p (g k) n", p=P), 8, 256))
    return units


def bank_uses():
    u = [("cond", 0), ("params", 1)]
    u += [(f"x{d}", (2 + d) % 8) for d in range(DT)]
    u += [("state_b0", 2), ("state_b1", 3), ("state_a", 4), ("ssq0", 5)]
    turn = [0]

    def tiles(labels):
        for label in labels:
            u.append((label, turn[0] % 6))
            turn[0] += 1

    for step in schedule():
        if step[0] == "ada":
            u.append((f"acc{step[1]}_{step[2]}", 7))
        elif step[0] == "in":
            tiles(f"in{step[1]}_{t}" for t in range(4))
        elif step[0] in ("out", "down"):
            tiles(f"{step[0]}{4 * step[1] + t}" for t in range(4))
        elif step[0] in ("gate", "up"):
            tiles(f"{step[0]}{t}" for t in ffn_tiles(step[1]))
        elif step[0] == "mid":
            tiles(["ln_sum", "ln_ssq", "new_a_prompt", "new_a_sample", "new_b_prompt", "new_b_sample"])
        elif step[0] == "norm1":
            tiles(["ssq1"])
        elif step[0] == "state_c":
            tiles(["state_c0", "state_c1"])
    tiles(["ssq2"])
    u += [(f"pool{d}", (d + 1) % 8) for d in range(DT)]
    u += [("new_c_prompt0", 2), ("new_c_prompt1", 3), ("new_c_sample0", 4), ("new_c_sample1", 5), ("ssq3", 6)]
    u += [("logits", 7)] + [(f"rows{t}{h}", 2 * t + h) for t in range(3) for h in range(2)]
    u += [("positions", 6), ("turned", 7)]
    u += [(f"pos{e}", e) for e in range(NE)] + [(f"wgt{e}", e) for e in range(NE)]
    seen, plan = [0] * 8, {}
    for label, b in u:
        seen[b] += 1
        plan[label] = (b, seen[b])
    return plan, seen


def build(nc, x_prompt, x_sample, state_a, state_b, state_c, c_prompt, c_sample, w_ada, b_ada, norm_mix,
          norm_ffn, norm_out, w_in, w_conv_a, w_conv_b, b_conv_b, ln_b_g, ln_b_b, w_out, w_ffn_gate,
          w_ffn_up, w_ffn_down, w_pool, pool_scale, w_router, b_router, w_exp_gate, w_exp_up, w_exp_down,
          y_prompt, y_sample, new_a_prompt, new_a_sample, new_b_prompt, new_b_sample, new_c_prompt,
          new_c_sample):
    units = weight_stream(w_ada, w_in, w_out, w_ffn_gate, w_ffn_up, w_ffn_down, w_pool)
    UNITS0 = len(units)
    assert EXPERT_UNITS % RING == 0
    plan, bank_total = bank_uses()

    with ExitStack() as ctx:
        def sb(name, shape, dt=F32):
            return ctx.enter_context(nc.sbuf_tensor(name, shape, dt))

        def sem(name):
            return ctx.enter_context(nc.semaphore(name))

        bank = [ctx.enter_context(nc.psum_tensor(f"bank{b}", [P, 512], F32)) for b in range(8)]
        filled = [sem(f"bank{b}_filled") for b in range(8)]
        emptied = [sem(f"bank{b}_emptied") for b in range(8)]

        ring = sb("ring", [P, RING, UNIT])
        ring_loaded = [sem(f"ring{s}_loaded") for s in range(RING)]
        ring_used = sem("ring_used")

        ROWS = sb("ROWS", [P, 3072])
        HT = sb("HT", [P, DT * NT])
        BIG = sb("BIG", [P, FT * NT])
        MIX = sb("MIX", [P, 4224])
        xT = sb("xT", [P, DT, NT])

        def cut(region, at, *dims):
            n = 1
            for m in dims:
                n *= m
            v = region[:, at:at + n]
            if len(dims) == 2:
                return v.rearrange("p (a b) -> p a b", a=dims[0])
            if len(dims) == 3:
                return v.rearrange("p (a b c) -> p a b c", a=dims[0], b=dims[1])
            return v

        x_rows = cut(ROWS, 0, 3, D)
        bada_rows = cut(BIG, 0, P)
        vec_rows = cut(BIG, 128, P)
        conv_b_rows = cut(BIG, 256, P)
        conv_a_rows = cut(BIG, 384, P)
        c_rows = cut(BIG, 512, D)
        state_b_rows = cut(BIG, 1536, 2, DA)
        state_a_rows = cut(BIG, 2560, DA)
        sq = cut(ROWS, 0, DT, NT)
        hT = cut(HT, 0, DT, NT)
        mixed = hT
        a_b = cut(BIG, 0, CT, NT)
        a_c = cut(BIG, CT * NT, CT, NT)
        a_x = cut(BIG, 2 * CT * NT, CT, NT)
        prod_b = cut(BIG, 3 * CT * NT, CT, NS, KB)
        gate_b = cut(BIG, 4 * CT * NT, CT, NT)
        tmp_a = cut(BIG, 5 * CT * NT, CT, NS, KA)
        up_a = cut(MIX, 0, CT, KA - 1 + NP)
        up_b = cut(MIX, 1032, CT, KB - 1 + NP)
        st_b = cut(MIX, 2176, CT, NS, KB)
        yb = cut(MIX, 3168, CT, NT)
        ada_part = cut(ROWS, DT * NT, BLK)
        new_rows = ROWS[0:KB - 1, 0:4 * DA].rearrange("p (s n) -> p s n", s=4)
        hid0 = cut(BIG, 0, FT, NT)
        sumA = cut(BIG, 0, DT, 16 + NP)
        sumB = cut(BIG, DT * (16 + NP), DT, 16 + NP)
        state_c_rows = cut(MIX, 0, D)
        st_c = cut(MIX, 1024, DT, NS, CTX)
        diff = cut(MIX, 2048, DT, NT)
        new_c_rows = ROWS[:, 0:2 * D].rearrange("p (s n) -> p s n", s=2)
        h_rows = cut(ROWS, 0, 3, D)
        xg = cut(HT, 0, DT, WIDE)
        hid = [cut(HT, DT * WIDE + b * 2 * WIDE, 2 * WIDE) for b in range(2)]
        outT = cut(MIX, 0, DT, WIDE)
        out_rows = cut(MIX, 1280, D)
        out_rows_b = cut(MIX, 2304, D)
        pick = cut(MIX, 3328, 3, WIDE)
        slot_row = cut(MIX, 3808, WIDE)
        posb = cut(BIG, 0, NE, NT)
        wgtb = cut(BIG, NE * NT, NE, NT)
        place = cut(BIG, 2 * NE * NT, NT)
        place_b = cut(BIG, 2 * NE * NT + NT, NT)
        sil = [cut(BIG, 2 * NE * NT + 2 * NT + b * 2 * WIDE, 2 * WIDE) for b in range(2)]
        beats = cut(BIG, 5392, 3, NE, NE)
        ties = cut(BIG, 5392 + 192, 3, NE, NE)
        y_rows = h_rows

        ident = sb("ident", [P, P])
        ones = sb("ones", [P, P])
        before = sb("before", [P, P])
        tri = sb("tri", [P, NE, NE])
        valid = sb("valid", [P, 3, NE])
        count_i = sb("count_i", [P, 16], I32)
        count = sb("count", [P, 16])
        share = sb("share", [P, 16])
        slot_i = sb("slot_i", [P, 4], I32)
        slot_col = sb("slot_col", [P, 2, 2])
        vec = sb("vec", [P, 292])
        bada = vec[:, 0:96].rearrange("p (l t) -> p l t", l=2)
        v_mix = vec[:, 96:112].rearrange("p (l t) -> p l t", l=2)
        v_ffn = vec[:, 112:128].rearrange("p (l t) -> p l t", l=2)
        v_out = vec[:, 128:136]
        v_bconv = vec[:, 136:140]
        v_lng = vec[:, 140:144]
        v_lnb = vec[:, 144:148]
        v_scale = vec[:, 148:156]
        v_conv_b = vec[:, 156:280].rearrange("p (k t) -> p t k", t=CT)
        v_conv_a = vec[:, 280:292].rearrange("p (k t) -> p t k", t=CT)
        csT = sb("csT", [P, DT, 32])
        pick_sum = sb("pick_sum", [P, NC])
        mod = sb("mod", [P, 2, 6 * DT, NC])
        gain = sb("gain", [P, 4, DT, NC])
        gate_s = sb("gate_s", [P, DT, NC])
        rstd = sb("rstd", [P, NT])
        ms = sb("ms", [P, NT])
        tmp8 = sb("tmp8", [P, DT, NS])
        st_a = sb("st_a", [P, CT, NS, KA])
        router = sb("router", [P, DT, NE])
        b_rt = sb("b_rt", [P, NE])
        lg = sb("lg", [P, 3, NE])
        pr = sb("pr", [P, 3, NE])
        stat = sb("stat", [P, 3])
        mask = sb("mask", [P, 3, NE])
        pm = sb("pm", [P, 3, 2 * NE])
        pmT = sb("pmT", [2 * NE, NT])
        pos_tab = sb("pos_tab", [P, 3, 2 * NE + 1])
        cnt = sb("cnt", [P, NE])
        flag_f = sb("flag_f", [P, 2 * NE + 2])
        flag = sb("flag", [P, 2 * NE + 2], I32)

        s = {}

        def on(name):
            if name not in s:
                s[name] = sem(name)
            return s[name]

        def shift_of(n):
            part = (n % 2) * 3
            return mod[:, n // 2, part * DT:(part + 1) * DT, :]

        def scale_of(n):
            part = (n % 2) * 3 + 1
            return mod[:, n // 2, part * DT:(part + 1) * DT, :]

        def gate_of(n):
            part = (n % 2) * 3 + 2
            return mod[:, n // 2, part * DT:(part + 1) * DT, :]

        block = ctx.enter_context(nc.Block())

        @block.sync
        def _(sp):
            sp.wait_ge(on("c_loaded"), 2 * 16)
            sp.wait_ge(on("x_loaded"), 2 * 16)
            sp.wait_ge(on("vec_loaded"), 10 * 16)
            for n, (src, kn, cols) in enumerate(units):
                if n >= RING:
                    sp.wait_ge(ring_used, n - RING + 1)
                dst = ring[:, n % RING, 0:kn * cols].rearrange("p (k n) -> p k n", k=kn)
                sp.dma_start(dst, src).then_inc(ring_loaded[n % RING], 16)

            def expert_units(e, base):
                n = 0

                def load(src, k):
                    nonlocal n
                    sp.wait_ge(ring_used, base + (UNITS0 - RING + 1 + n))
                    slot = (UNITS0 + n) % RING
                    sp.dma_start(ring[:, slot, :].rearrange("p (k n) -> p k n", k=k), src).then_inc(ring_loaded[slot], 16)
                    n += 1

                gate_v = w_exp_gate[0].rearrange("e (h k p) f -> e h p k f", h=KH, p=P)
                up_v = w_exp_up[0].rearrange("e (h k p) f -> e h p k f", h=KH, p=P)
                down_v = w_exp_down[0].rearrange("e (q k p) d -> e q p k d", q=PAIRS, p=P)
                for c in range(CHUNKS):
                    for v in (gate_v, up_v):
                        for h in range(KH):
                            load(v[e, h, :, :, c * BLK:(c + 1) * BLK], 4)
                    if c:
                        load(down_v[e, 2 * c - 1], 2)
                    load(down_v[e, 2 * c], 2)
                load(down_v[e, PAIRS - 1], 2)

            with sp.Fori(0, NE) as e:
                expert_units(e, e * EXPERT_UNITS)
            sp.wait_ge(on("flags_ready"), 1)
            passes = sp.value_load(flag[0:1, 2 * NE + 1:2 * NE + 2], min_val=1, max_val=2)
            with sp.If(passes == 2):
                with sp.Fori(0, NE) as e:
                    expert_units(e, (e + NE) * EXPERT_UNITS)

        @block.gpsimd
        def _(pool):
            g = nc.gpsimd
            chain = [0]

            def link(ins):
                chain[0] += 1
                ins.then_inc(on("pool_chain"), 1)
                pool.wait_ge(on("pool_chain"), chain[0])

            g.memset(ones[:], 1.0)
            g.memset(ident[:], 0.0)
            g.memset(tri[:], 1.0)
            g.memset(valid[:], 1.0)
            g.memset(flag_f[:], 0.0)
            g.memset(pos_tab[:], -1.0)
            g.memset(lg[:], 0.0)
            g.memset(csT[:], 0.0)
            link(g.memset(before[:], 1.0))
            g.affine_select(out=ident[:], in_=ident[:], compare_op=ALU.not_equal, fill=1.0, base=0,
                            pattern=[[-1, P]], channel_multiplier=1)
            g.affine_select(out=before[:], in_=before[:], compare_op=ALU.is_gt, fill=0.0, base=0,
                            pattern=[[1, P]], channel_multiplier=-1)
            g.affine_select(out=tri[:], in_=tri[:], compare_op=ALU.is_gt, fill=0.0, base=0,
                            pattern=[[1, NE], [-1, NE]], channel_multiplier=0)
            g.affine_select(out=valid[:, 2, :], in_=valid[:, 2, :], compare_op=ALU.is_gt, fill=0.0, base=NS,
                            pattern=[[0, NE]], channel_multiplier=-1)
            g.iota(slot_i[:], [[WIDE, 2], [P, 2]], base=0, channel_multiplier=1)
            link(g.iota(count_i[:], [[1, 16]], base=1, channel_multiplier=0))
            g.tensor_copy(slot_col[:].rearrange("p a b -> p (a b)"), slot_i[:])
            g.tensor_copy(count[:], count_i[:])
            link(g.tensor_tensor(pick_sum[:], ident[:, 0:NC], ident[:, 32:32 + NC], ALU.add))
            link(g.tensor_tensor(pick_sum[:], pick_sum[:], ident[:, 64:64 + NC], ALU.add))
            g.tensor_tensor(pick_sum[:], pick_sum[:], ident[:, 96:96 + NC], ALU.add).then_inc(on("consts_ready"), 1)
            g.memset(up_a[:, :, 0:KA - 1], 0.0)
            g.memset(up_b[:, :, 0:KB - 1], 0.0).then_inc(on("pads_ready"), 1)

            def sample_mod(n):
                pool.wait_ge(on("rstd_ready"), n + 1)
                pool.wait_ge(on("gain_ready"), n + 1)
                hs = hT[:, :, NP:NT]
                link(g.tensor_tensor(hs, xT[:, :, NP:NT], gain[:, n, :, 1:NC], ALU.mult))
                link(g.tensor_tensor(hs, hs, rstd[:, NP:NT].unsqueeze(1).to_broadcast([P, DT, NS]), ALU.mult))
                g.tensor_tensor(hs, hs, shift_of(n)[:, :, 1:NC], ALU.add).then_inc(on("hs_ready"), 1)

            sample_mod(0)
            pool.wait_ge(on("a_copied"), 2 * CT)
            link(g.tensor_tensor(up_a[:, :, KA - 1:], a_c[:, :, 0:NP], a_x[:, :, 0:NP], ALU.mult))
            pool.wait_ge(on("state_a_ready"), 1)
            link(g.tensor_tensor(st_a[:, :, :, KA - 1], a_c[:, :, NP:NT], a_x[:, :, NP:NT], ALU.mult))
            pool.sem_inc(on("up_a_ready"), 1)
            for k in range(KA):
                tap = v_conv_a[:, :, k:k + 1].to_broadcast([P, CT, NP])
                dst = a_x if k else a_c
                link(g.tensor_tensor(dst[:, :, 0:NP], up_a[:, :, k:k + NP], tap, ALU.mult))
                if k:
                    link(g.tensor_tensor(a_c[:, :, 0:NP], a_c[:, :, 0:NP], a_x[:, :, 0:NP], ALU.add))
            taps = v_conv_a[:, :, :].unsqueeze(2).to_broadcast([P, CT, NS, KA])
            link(g.tensor_tensor(tmp_a, st_a[:], taps, ALU.mult))
            link(g.tensor_tensor(a_c[:, :, NP:NT], tmp_a[:, :, :, 0], tmp_a[:, :, :, 1], ALU.add))
            link(g.tensor_tensor(a_c[:, :, NP:NT], a_c[:, :, NP:NT], tmp_a[:, :, :, 2], ALU.add))
            pool.wait_ge(on("a_copied"), 3 * CT)
            g.tensor_tensor(mixed[:, 0:CT, :], a_b, a_c, ALU.mult).then_inc(on("ya_ready"), 1)
            sample_mod(1)
            sample_mod(2)
            sample_mod(3)
            pool.wait_ge(filled[plan["pool7"][0]], plan["pool7"][1])
            g.iota(slot_row.bitcast(I32), [[1, WIDE]], base=0, channel_multiplier=0).then_inc(on("slots_i"), 1)
            pool.wait_ge(on("slots_i"), 1)
            g.tensor_copy(slot_row, slot_row.bitcast(I32)).then_inc(on("slots_ready"), 1)

        @block.scalar
        def _(act):
            a = nc.scalar
            chain = [0]

            def link(ins):
                chain[0] += 1
                ins.then_inc(on("act_chain"), 1)
                act.wait_ge(on("act_chain"), chain[0])

            def wait_bank(label):
                b, n = plan[label]
                act.wait_ge(filled[b], n)
                return bank[b]

            def empty(label, ins):
                ins.then_inc(emptied[plan[label][0]], 1)

            def landed(label):
                act.wait_ge(emptied[plan[label][0]], plan[label][1])

            act.dma_start(c_rows[0:1, :], c_prompt).then_inc(on("c_loaded"), 16)
            act.dma_start(c_rows[1:NC, :], c_sample).then_inc(on("c_loaded"), 16)
            act.dma_start(x_rows[:, 0:2, :], x_prompt[0].rearrange("(t p) d -> p t d", p=P)).then_inc(on("x_loaded"), 16)
            act.dma_start(x_rows[0:NS, 2, :], x_sample[:, 0, :]).then_inc(on("x_loaded"), 16)
            act.dma_start(bada_rows[0:96, :], b_ada.rearrange("l (t p) -> (l t) p", p=P)).then_inc(on("vec_loaded"), 16)
            at = 0
            for v in (norm_mix.rearrange("l (t p) -> (l t) p", p=P), norm_ffn.rearrange("l (t p) -> (l t) p", p=P),
                      norm_out.rearrange("(t p) -> t p", p=P), b_conv_b[0].rearrange("(t p) -> t p", p=P),
                      ln_b_g[0].rearrange("(t p) -> t p", p=P), ln_b_b[0].rearrange("(t p) -> t p", p=P),
                      pool_scale[0].rearrange("(t p) -> t p", p=P)):
                n = v.shape[0]
                act.dma_start(vec_rows[at:at + n, :], v).then_inc(on("vec_loaded"), 16)
                at += n
            act.dma_start(conv_b_rows[0:KB * CT, :], w_conv_b[0].rearrange("k (t p) -> (k t) p", p=P)).then_inc(on("vec_loaded"), 16)
            act.dma_start(conv_a_rows[0:KA * CT, :], w_conv_a[0].rearrange("k (t p) -> (k t) p", p=P)).then_inc(on("vec_loaded"), 16)
            act.dma_start(state_b_rows[0:120, :, :], state_b[0].rearrange("b k d -> (b k) d").rearrange("(s p) d -> p s d", p=120)).then_inc(on("states_loaded"), 16)
            act.dma_start(state_a_rows[0:2 * NS, :], state_a[0].rearrange("b k d -> (b k) d")).then_inc(on("states_loaded"), 16)
            act.dma_start(router[:], w_router[0].rearrange("(k p) e -> p k e", p=P)).then_inc(on("router_loaded"), 16)
            act.dma_start(b_rt[:], b_router.to_broadcast([P, NE])).then_inc(on("router_loaded"), 16)
            act.dma_start(new_a_sample[0, :, 0:1, :], state_a[0, :, 1:2, :]).then_inc(on("stored"), 16)
            act.dma_start(new_b_sample[0, :, 0:KB - 2, :], state_b[0, :, 1:KB - 1, :]).then_inc(on("stored"), 16)
            act.dma_start(new_c_sample[0, :, 0:CTX - 1, :], state_c[0, :, 1:CTX, :]).then_inc(on("stored"), 16)

            act.wait_ge(on("consts_ready"), 1)
            empty("cond", a.activation(csT[:, :, 0:NC], wait_bank("cond")[:, 0:DT * NC].rearrange("p (t c) -> p t c", c=NC),
                                       ACT.Silu))
            for d in range(1, DT, 2):
                empty(f"x{d}", a.activation(xT[:, d, :], wait_bank(f"x{d}")[:, 0:NT], ACT.Copy))
            landed(f"x{DT - 1}")
            act.sem_inc(on("x_odd"), 1)

            def squares(n):
                act.wait_ge(on("x_ready"), n + 1)
                a.activation(sq.rearrange("p t n -> p (t n)"), xT[:].rearrange("p t n -> p (t n)"),
                             ACT.Square).then_inc(on("sq_ready"), 1)
                act.wait_ge(on("recip_ready"), n + 1)
                a.activation(rstd[:], ms[:], ACT.Sqrt).then_inc(on("rstd_ready"), 1)

            def shifts(n):
                for d in range(DT):
                    act.wait_ge(on("scaled"), n * DT + d + 1)
                    a.activation(hT[:, d, 0:NP], hT[:, d, 0:NP], ACT.Identity,
                                 bias=shift_of(n)[:, d, 0:1]).then_inc(on("h_ready"), 1)

            squares(0)
            for j in range(2):
                src = wait_bank(f"state_b{j}")[:, 0:480].rearrange("p (t b k) -> p t b k", t=2, b=NS)
                for t in range(2):
                    ins = a.activation(st_b[:, 2 * j + t, :, 0:KB - 1], src[:, t], ACT.Copy)
                empty(f"state_b{j}", ins)
            for t in range(CT):
                src = wait_bank("state_a")[:, 0:64].rearrange("p (t b k) -> p t b k", t=CT, b=NS)
                ins = a.activation(st_a[:, t, :, 0:KA - 1], src[:, t], ACT.Copy)
            empty("state_a", ins)
            landed("state_a")
            act.sem_inc(on("state_a_ready"), 1)

            def ada_copy(layer, blk):
                if layer or blk:
                    act.wait_ge(on("ada_turned"), layer * 2 * HALF_BLOCKS + blk)
                label = f"acc{layer}_{blk}"
                empty(label, a.activation(ada_part, wait_bank(label)[:], ACT.Copy))

            for blk in range(HALF_BLOCKS):
                ada_copy(0, blk)
            shifts(0)
            in_dst = {1: a_c, 2: a_x, 0: a_b}
            for step in schedule()[HALF_BLOCKS:]:
                if step[0] == "mid":
                    break
                if step[0] == "ada":
                    ada_copy(*step[1:])
                elif step[1] == 4:
                    for t in range(CT):
                        empty(f"in4_{t}", a.activation(gate_b[:, t, :], wait_bank(f"in4_{t}")[:, 0:NT], ACT.Sigmoid))
                        landed(f"in4_{t}")
                    act.sem_inc(on("gate_b_ready"), 1)
                elif step[1] in in_dst:
                    for t in range(CT):
                        label = f"in{step[1]}_{t}"
                        empty(label, a.activation(in_dst[step[1]][:, t, :], wait_bank(label)[:, 0:NT], ACT.Copy))
                        landed(label)
                        act.sem_inc(on("a_copied"), 1)
            act.wait_ge(on("centred"), CT)
            a.activation(gate_b, yb, ACT.Square).then_inc(on("ln_sq_ready"), 1)
            act.wait_ge(on("ln_recip_ready"), 1)
            a.activation(rstd[:], ms[:], ACT.Sqrt).then_inc(on("ln_rstd_ready"), 1)
            for t in range(CT):
                act.wait_ge(on("ln_scaled"), t + 1)
                a.activation(mixed[:, CT + t, :], yb[:, t, :], ACT.Silu, bias=v_lnb[:, t:t + 1],
                             scale=v_lng[:, t:t + 1]).then_inc(on("yb_ready"), 1)
            for i, (label, rows, dst) in enumerate((
                    ("new_a_prompt", KA - 1, new_a_prompt[0, 0]), ("new_a_sample", NS, new_a_sample[0, :, KA - 2, :]),
                    ("new_b_prompt", KB - 1, new_b_prompt[0, 0]), ("new_b_sample", NS, new_b_sample[0, :, KB - 2, :]))):
                b, n = plan[label]
                empty(label, a.activation(new_rows[0:rows, i, :], wait_bank(label)[0:rows, :], ACT.Copy))
                act.wait_ge(emptied[b], n)
                act.dma_start(dst, new_rows[0:rows, i, :]).then_inc(on("new_stored"), 16)
            act.wait_ge(on("new_stored"), 4 * 16)
            squares(1)
            shifts(1)
            act.dma_start(state_c_rows[0:NS * CTX, :], state_c[0].rearrange("b k d -> (b k) d")).then_inc(on("state_c_loaded"), 16)
            for i in range(FFN_STEPS):
                for t in ffn_tiles(i):
                    empty(f"gate{t}", a.activation(hid0[:, t, :], wait_bank(f"gate{t}")[:, 0:NT], ACT.Silu))
                for blk in (2 * i, 2 * i + 1):
                    ada_copy(1, blk)
            for j in range(2):
                src = wait_bank(f"state_c{j}")[:, 0:480].rearrange("p (t b k) -> p (t b) k", t=4, b=NS)
                dst = st_c[:, 4 * j:4 * j + 4].rearrange("p t b k -> p (t b) k")
                empty(f"state_c{j}", a.activation(dst, src, ACT.Copy))
            squares(2)
            shifts(2)
            for i, (what, rows) in enumerate((("prompt", CTX), ("sample", NS))):
                for j in range(2):
                    label = f"new_c_{what}{j}"
                    b, n = plan[label]
                    empty(label, a.activation(new_c_rows[0:rows, i, j * 512:(j + 1) * 512],
                                              wait_bank(label)[0:rows, :], ACT.Copy))
                    act.wait_ge(emptied[b], n)
            act.dma_start(new_c_prompt[0, 0], new_c_rows[0:CTX, 0, :]).then_inc(on("new_stored"), 16)
            act.dma_start(new_c_sample[0, :, CTX - 1, :], new_c_rows[0:NS, 1, :]).then_inc(on("new_stored"), 16)
            act.wait_ge(on("new_stored"), 6 * 16)
            squares(3)
            shifts(3)
            for t in range(3):
                n = TILES[t][1]
                label = f"rows{t}0"
                empty(label, a.activation(h_rows[0:n, t, 0:512], wait_bank(label)[0:n, :], ACT.Copy))
            landed("rows20")
            act.sem_inc(on("rows_even"), 1)
            act.wait_ge(on("centred_logits"), 1)
            a.activation(pr[:], lg[:], ACT.Exp).then_inc(on("exp_ready"), 1)

            act.wait_ge(on("flags_ready"), 1)
            passes = act.value_load(flag[0:1, 2 * NE + 1:2 * NE + 2], min_val=1, max_val=2)

            def expert_scalar(q, w):
                for p in range(PAIRS):
                    act.wait_ge(on("gate_done"), q * PAIRS + (p + 1))
                    if p >= 2:
                        act.wait_ge(on("hid_ready"), q * PAIRS + (p - 1))
                    a.activation(sil[p % 2][:, 0:2 * w], bank[2 * (p % 2)][:, 0:2 * w],
                                 ACT.Silu).then_inc(on("silu_ready"), 1)
                act.wait_ge(on("out_done"), q + 1)
                for b, d0, dn in ((4, 0, 3), (5, 3, 3), (6, 6, 2)):
                    ins = a.activation(outT[:, d0:d0 + dn, 0:w],
                                       bank[b][:, 0:dn * w].rearrange("p (t n) -> p t n", t=dn), ACT.Copy)
                ins.then_inc(on("outT_ready"), 1)
                act.wait_ge(on("turned_out"), q + 1)
                m = min(w, P)
                ins = a.activation(out_rows[0:m, 0:512], bank[7][0:m, :], ACT.Copy)
                if w > P:
                    a.activation(out_rows_b[0:w - P, 0:512], bank[5][0:w - P, :], ACT.Copy)
                    a.activation(out_rows_b[0:w - P, 512:1024], bank[6][0:w - P, :], ACT.Copy)
                a.activation(out_rows[0:m, 512:1024], bank[4][0:m, :], ACT.Copy).then_inc(on("out_rows_ready"), 1)

            with act.Fori(0, passes) as ps:
                with act.Fori(0, NE) as e:
                    q = ps * NE + e
                    wide = act.value_load(flag[0:1, bass.ds(q, 1)], min_val=0, max_val=1)
                    with act.If(wide == 1):
                        expert_scalar(q, WIDE)
                    with act.Else():
                        expert_scalar(q, NARROW)

            squares(4)
            for t in range(3):
                n = TILES[t][1]
                act.wait_ge(on("y_turned"), 2 * t + 1)
                a.activation(y_rows[0:n, t, 0:512], bank[2 * t][0:n, :], ACT.Copy).then_inc(on("y_copied_a"), 1)
                act.wait_ge(on("y_copied_a"), t + 1)
                act.wait_ge(on("y_copied_v"), t + 1)
                dst = y_sample[:, 0, :] if t == 2 else y_prompt[0, t * P:(t + 1) * P, :]
                act.dma_start(dst, y_rows[0:n, t, :]).then_inc(on("y_stored"), 16)
            act.wait_ge(on("stored"), 3 * 16)
            act.wait_ge(on("new_stored"), 6 * 16)
            act.wait_ge(on("y_stored"), 3 * 16)

        @block.vector
        def _(dve):
            v = nc.vector
            chain = [0]

            def link(ins):
                chain[0] += 1
                ins.then_inc(on("dve_chain"), 1)
                dve.wait_ge(on("dve_chain"), chain[0])

            def wait_bank(label):
                b, n = plan[label]
                dve.wait_ge(filled[b], n)
                return bank[b]

            def empty(label, ins):
                ins.then_inc(emptied[plan[label][0]], 1)

            def landed(label):
                dve.wait_ge(emptied[plan[label][0]], plan[label][1])

            dve.sem_inc(on("x_updated"), DT)
            empty("params", v.tensor_copy(vec[:], wait_bank("params")[:, 0:292]))
            landed("params")
            for d in range(0, DT, 2):
                empty(f"x{d}", v.tensor_copy(xT[:, d, :], wait_bank(f"x{d}")[:, 0:NT]))
            landed("x6")
            dve.wait_ge(on("x_odd"), 1)
            dve.sem_inc(on("x_ready"), 1)

            def make_gain(n, norm):
                v.scalar_tensor_tensor(gain[:, n], scale_of(n), 1.0, norm.unsqueeze(2).to_broadcast([P, DT, NC]),
                                       ALU.add, ALU.mult).then_inc(on("gain_ready"), 1)
                dve.wait_ge(on("gain_ready"), n + 1)

            def add_ada(layer, half):
                n = 2 * layer + half + 1
                t0 = half * 3 * DT
                dve.wait_ge(on("ada_turned"), n * HALF_BLOCKS)
                src = bank[6][:, 0:3 * DT * NC].rearrange("p (t c) -> p t c", c=NC)
                v.tensor_tensor(mod[:, layer, t0:t0 + 3 * DT, :], src,
                                bada[:, layer, t0:t0 + 3 * DT].unsqueeze(2).to_broadcast([P, 3 * DT, NC]),
                                ALU.add).then_inc(on("ada_taken"), 1)
                dve.wait_ge(on("ada_taken"), n)

            def mean_square(n):
                label = f"ssq{n}"
                if n < 4:
                    src = wait_bank(label)
                else:
                    dve.wait_ge(on("ssq_final"), 1)
                    src = bank[0]
                ins = v.tensor_scalar(ms[:], src[:, 0:NT], 1.0 / D, EPS, ALU.mult, ALU.add)
                if n < 4:
                    empty(label, ins)
                    landed(label)
                else:
                    link(ins)
                v.reciprocal(ms[:], ms[:]).then_inc(on("recip_ready"), 1)
                dve.wait_ge(on("rstd_ready"), n + 1)

            def scaled(n):
                for d in range(DT):
                    v.scalar_tensor_tensor(hT[:, d, 0:NP], xT[:, d, 0:NP], gain[:, n, d, 0:1], rstd[:, 0:NP],
                                           ALU.mult, ALU.mult).then_inc(on("scaled"), 1)

            def residual(d, src, g):
                v.scalar_tensor_tensor(xT[:, d, 0:NP], src[:, 0:NP], g[:, d, 0:1], xT[:, d, 0:NP], ALU.mult, ALU.add)
                return v.tensor_tensor(tmp8[:, d, :], src[:, NP:NT], g[:, d, 1:NC], ALU.mult)

            def add_samples():
                return v.tensor_tensor(xT[:, :, NP:NT], xT[:, :, NP:NT], tmp8[:], ALU.add)

            def block_residual(name, g):
                for d in range(DT):
                    label = f"{name}{d}"
                    empty(label, residual(d, wait_bank(label), g))
                landed(f"{name}{DT - 1}")
                add_samples().then_inc(on("x_ready"), 1)

            mean_square(0)
            add_ada(0, 0)
            make_gain(0, v_mix[:, 0])
            scaled(0)
            dve.wait_ge(on("pads_ready"), 1)
            dve.wait_ge(on("gate_b_ready"), 1)
            for t in range(CT):
                label = f"in3_{t}"
                src = wait_bank(label)
                v.tensor_tensor(up_b[:, t, KB - 1:], src[:, 0:NP], gate_b[:, t, 0:NP], ALU.mult)
                empty(label, v.tensor_tensor(st_b[:, t, :, KB - 1], src[:, NP:NT], gate_b[:, t, NP:NT], ALU.mult))
                landed(label)
            dve.sem_inc(on("up_b_ready"), 1)
            taps = 0
            for k in range(KB):
                for t in range(CT):
                    src = up_b[:, t, k:k + NP]
                    if k:
                        dve.wait_ge(on("tap_done"), taps - CT + 1)
                        ins = v.scalar_tensor_tensor(yb[:, t, 0:NP], src, v_conv_b[:, t, k:k + 1], yb[:, t, 0:NP],
                                                     ALU.mult, ALU.add)
                    else:
                        ins = v.tensor_scalar(yb[:, t, 0:NP], src, v_conv_b[:, t, 0:1], v_bconv[:, t:t + 1],
                                              ALU.mult, ALU.add)
                    ins.then_inc(on("tap_done"), 1)
                    taps += 1
            link(v.tensor_tensor(prod_b, st_b, v_conv_b.unsqueeze(2).to_broadcast([P, CT, NS, KB]), ALU.mult))
            for t in range(CT):
                ins = v.tensor_reduce(yb[:, t, NP:NT], prod_b[:, t], AX_X, ALU.add)
            link(ins)
            v.tensor_tensor(yb[:, :, NP:NT], yb[:, :, NP:NT], v_bconv.unsqueeze(2).to_broadcast([P, CT, NS]),
                            ALU.add).then_inc(on("conv_b_done"), 1)
            add_ada(0, 1)
            make_gain(1, v_ffn[:, 0])
            src = wait_bank("ln_sum")
            for t in range(CT):
                ins = v.scalar_tensor_tensor(yb[:, t, :], src[:, 0:NT], -1.0 / DA, yb[:, t, :], ALU.mult, ALU.add)
                if t < CT - 1:
                    ins.then_inc(on("centred"), 1)
            empty("ln_sum", ins)
            landed("ln_sum")
            dve.sem_inc(on("centred"), 1)
            empty("ln_ssq", v.tensor_scalar(ms[:], wait_bank("ln_ssq")[:, 0:NT], 1.0 / DA, EPS, ALU.mult, ALU.add))
            landed("ln_ssq")
            v.reciprocal(ms[:], ms[:]).then_inc(on("ln_recip_ready"), 1)
            dve.wait_ge(on("ln_rstd_ready"), 1)
            for t in range(CT):
                v.tensor_tensor(yb[:, t, :], yb[:, t, :], rstd[:], ALU.mult).then_inc(on("ln_scaled"), 1)
            block_residual("out", gate_of(0))
            mean_square(1)
            scaled(1)
            for i in range(FFN_STEPS):
                for t in ffn_tiles(i):
                    label = f"up{t}"
                    src = wait_bank(label)
                    gb, gn = plan[f"gate{t}"]
                    dve.wait_ge(emptied[gb], gn)
                    empty(label, v.tensor_tensor(hid0[:, t, :], src[:, 0:NT], hid0[:, t, :], ALU.mult))
                if 2 * (i + 1) == HALF_BLOCKS:
                    add_ada(1, 0)
                    make_gain(2, v_mix[:, 1])
                    link(v.tensor_tensor(gate_s[:], gate_of(2), v_scale.unsqueeze(2).to_broadcast([P, DT, NC]), ALU.mult))
            add_ada(1, 1)
            make_gain(3, v_ffn[:, 1])
            block_residual("down", gate_of(1))
            mean_square(2)
            link(v.memset(BIG[:, 0:2 * DT * (16 + NP)], 0.0))
            scaled(2)
            v.reciprocal(share[:], count[:])
            dve.wait_ge(on("h_ready"), 3 * DT)
            dve.wait_ge(on("hs_ready"), 3)
            v.tensor_copy(sumA[:, :, 16:17], hT[:, :, 0:1])
            link(v.tensor_tensor(sumA[:, :, 17:], hT[:, :, 1:NP], hT[:, :, 0:NP - 1], ALU.add))
            bufs = (sumA, sumB)
            for i, w in enumerate(WINDOWS[:-1]):
                src, dst = bufs[i % 2], bufs[(i + 1) % 2]
                d0 = 2 * (i + 1)
                link(v.tensor_tensor(dst[:, d0:, 16:], src[:, d0:, 16:], src[:, d0:, 16 - w:16 - w + NP], ALU.add))
            for i, w in enumerate(WINDOWS):
                src = bufs[i % 2][:, 2 * i:2 * i + 2, 16:]
                h = hT[:, 2 * i:2 * i + 2, :]
                out = diff[:, 2 * i:2 * i + 2, :]
                if w > 1:
                    v.tensor_tensor(out[:, :, 0:w - 1], src[:, :, 0:w - 1],
                                    share[:, 0:w - 1].unsqueeze(1).to_broadcast([P, 2, w - 1]), ALU.mult)
                v.scalar_tensor_tensor(out[:, :, w - 1:NP], src[:, :, w - 1:], 1.0 / w, h[:, :, w - 1:NP],
                                       ALU.mult, ALU.subtract)
                st = st_c[:, 2 * i:2 * i + 2, :, CTX - (w - 1):].rearrange("p t b k -> p (t b) k")
                link(v.tensor_reduce(tmp8[:, 2 * i:2 * i + 2, :].rearrange("p t b -> p (t b)"), st, AX_X, ALU.add))
                link(v.tensor_tensor(tmp8[:, 2 * i:2 * i + 2, :], tmp8[:, 2 * i:2 * i + 2, :], h[:, :, NP:NT], ALU.add))
                v.tensor_tensor(out[:, :, 0:w - 1], out[:, :, 0:w - 1], h[:, :, 0:w - 1], ALU.subtract)
                v.scalar_tensor_tensor(out[:, :, NP:NT], tmp8[:, 2 * i:2 * i + 2, :], 1.0 / w, h[:, :, NP:NT],
                                       ALU.mult, ALU.subtract).then_inc(on("diff_ready"), 1)
            dve.wait_ge(on("diff_ready"), 4)
            block_residual("pool", gate_s)
            mean_square(3)
            scaled(3)
            src = wait_bank("logits")
            brt = b_rt[:].unsqueeze(1).to_broadcast([P, 2, NE])
            dve.wait_ge(on("router_loaded"), 2 * 16)
            v.tensor_tensor(lg[:, 0:2, :], src[:, 0:2 * NE].rearrange("p (t e) -> p t e", e=NE), brt, ALU.add)
            empty("logits", v.tensor_tensor(lg[0:NS, 2, :], src[0:NS, 2 * NE:3 * NE], b_rt[0:NS, :], ALU.add))
            landed("logits")
            wide3 = stat[:].unsqueeze(2).to_broadcast([P, 3, NE])
            link(v.tensor_reduce(stat[:], lg[:], AX_X, ALU.max))
            v.tensor_tensor(lg[:], lg[:], wide3, ALU.subtract).then_inc(on("centred_logits"), 1)
            for t in range(3):
                n = TILES[t][1]
                label = f"rows{t}1"
                empty(label, v.tensor_copy(h_rows[0:n, t, 512:1024], wait_bank(label)[0:n, :]))
            dve.wait_ge(on("exp_ready"), 1)
            link(v.tensor_reduce(stat[:], pr[:], AX_X, ALU.add))
            link(v.reciprocal(stat[:], stat[:]))
            link(v.tensor_tensor(pr[:], pr[:], wide3, ALU.mult))
            for t in range(3):
                mine = pr[:, t, :].unsqueeze(2).to_broadcast([P, NE, NE])
                other = pr[:, t, :].unsqueeze(1).to_broadcast([P, NE, NE])
                v.tensor_tensor(beats[:, t], other, mine, ALU.is_gt)
                ins = v.tensor_tensor(ties[:, t], other, mine, ALU.is_equal)
            link(ins)
            link(v.tensor_tensor(ties, ties, tri[:].unsqueeze(1).to_broadcast([P, 3, NE, NE]), ALU.mult))
            link(v.tensor_tensor(beats, beats, ties, ALU.add))
            link(v.tensor_reduce(mask[:], beats, AX_X, ALU.add))
            link(v.scalar_tensor_tensor(mask[:], mask[:], 2.0, valid[:], ALU.is_lt, ALU.mult))
            dve.sem_inc(on("mask_ready"), 1)
            link(v.tensor_tensor(pr[:], pr[:], mask[:], ALU.mult))
            link(v.tensor_reduce(stat[:], pr[:], AX_X, ALU.add))
            link(v.scalar_tensor_tensor(stat[:], valid[:, :, 0], 1.0, stat[:], ALU.is_lt, ALU.add))
            link(v.reciprocal(stat[:], stat[:]))
            link(v.tensor_tensor(pm[:, :, NE:2 * NE], pr[:], wide3, ALU.mult))
            src = wait_bank("positions")
            link(v.scalar_tensor_tensor(pm[:, :, 0:NE], src[:, 0:3 * NE].rearrange("p (t e) -> p t e", e=NE), 1.0,
                                        mask[:], ALU.add, ALU.mult))
            empty("positions", v.tensor_copy(cnt[:], src[:, 3 * NE:4 * NE]))
            landed("positions")
            v.tensor_scalar(pm[:, :, 0:NE], pm[:, :, 0:NE], -1.0, None, ALU.add).then_inc(on("pm_ready"), 1)
            v.tensor_scalar(flag_f[:, 0:NE], cnt[:], float(NARROW), None, ALU.is_gt)
            v.tensor_scalar(flag_f[:, NE:2 * NE], cnt[:], float(WIDE + NARROW), None, ALU.is_gt)
            link(v.tensor_reduce(stat[:, 0:1], cnt[:], AX_X, ALU.max))
            link(v.tensor_scalar(flag_f[:, 2 * NE + 1:2 * NE + 2], stat[:, 0:1], float(WIDE), 1.0, ALU.is_gt, ALU.add))
            v.tensor_copy(flag[:], flag_f[:]).then_inc(on("flags_ready"), 1)
            dve.wait_ge(on("pm_ready"), 1)
            v.tensor_copy(pos_tab[:, :, 0:NE], pm[:, :, 0:NE])
            link(v.tensor_scalar(pos_tab[:, :, NE:2 * NE], pm[:, :, 0:NE], -float(WIDE), None, ALU.add))

            def pick_matrix(q):
                for t in range(3):
                    n = TILES[t][1]
                    ins = v.tensor_scalar(pick[0:n, t, :], slot_row[0:n, :], pos_tab[0:n, t, bass.ds(q, 1)], None,
                                          ALU.is_equal)
                ins.then_inc(on("pick_ready"), 1)

            def take_batch(q, w):
                for b in range(4):
                    dve.wait_ge(on("gathered"), q * 4 + (b + 1))
                    v.tensor_copy(xg[:, 2 * b:2 * b + 2, 0:w],
                                  bank[b][:, 0:2 * w].rearrange("p (t n) -> p t n", t=2)).then_inc(on("xg_ready"), 1)

            dve.wait_ge(on("slots_ready"), 1)
            pick_matrix(0)
            empty("turned", v.tensor_copy(pmT[:], wait_bank("turned")[0:2 * NE, 0:NT]))
            landed("turned")
            dve.sem_inc(on("pmT_ready"), 1)
            for kind, dst in (("pos", posb), ("wgt", wgtb)):
                for e in range(NE):
                    label = f"{kind}{e}"
                    empty(label, v.tensor_copy(dst[:, e, :], wait_bank(label)[:, 0:NT]))
            landed(f"wgt{NE - 1}")
            dve.wait_ge(on("flags_ready"), 1)
            passes = dve.value_load(flag[0:1, 2 * NE + 1:2 * NE + 2], min_val=1, max_val=2)
            wide = dve.value_load(flag[0:1, 0:1], min_val=0, max_val=1)
            with dve.If(wide == 1):
                take_batch(0, WIDE)
            with dve.Else():
                take_batch(0, NARROW)

            def expert_vector(q, w):
                for p in range(PAIRS):
                    dve.wait_ge(on("silu_ready"), q * PAIRS + (p + 1))
                    dve.wait_ge(on("up_done"), q * PAIRS + (p + 1))
                    v.tensor_tensor(hid[p % 2][:, 0:2 * w], bank[2 * (p % 2) + 1][:, 0:2 * w], sil[p % 2][:, 0:2 * w],
                                    ALU.mult).then_inc(on("hid_ready"), 1)

            with dve.Fori(0, passes) as ps:
                with dve.Fori(0, NE) as e:
                    q = ps * NE + e
                    for dst, half in ((place, 0), (place_b, 1)):
                        m = P if half == 0 else WIDE - P
                        v.scalar_tensor_tensor(dst[0:m, :], posb[0:m, bass.ds(e, 1), :].rearrange("p o n -> p (o n)"),
                                               slot_col[0:m, bass.ds(ps, 1), half:half + 1].rearrange("p a b -> p (a b)"),
                                               wgtb[0:m, bass.ds(e, 1), :].rearrange("p o n -> p (o n)"),
                                               ALU.is_equal, ALU.mult).then_inc(on("place_ready"), 1)
                    pick_matrix(q + 1)
                    wide = dve.value_load(flag[0:1, bass.ds(q, 1)], min_val=0, max_val=1)
                    with dve.If(wide == 1):
                        expert_vector(q, WIDE)
                    with dve.Else():
                        expert_vector(q, NARROW)
                    wide_next = dve.value_load(flag[0:1, bass.ds(q + 1, 1)], min_val=0, max_val=1)
                    with dve.If(wide_next == 1):
                        take_batch(q + 1, WIDE)
                    with dve.Else():
                        take_batch(q + 1, NARROW)
                    for d in range(DT):
                        dve.wait_ge(on("scattered"), q * DT + (d + 1))
                        residual(d, bank[(7, 4, 5, 6)[d % 4]], gate_of(3)).then_inc(on("x_updated"), 1)
                    dve.wait_ge(on("x_updated"), q * DT + 2 * DT)
                    add_samples().then_inc(on("samples_added"), 1)
                    dve.wait_ge(on("samples_added"), q + 1)

            dve.sem_inc(on("x_ready"), 1)
            mean_square(4)
            for d in range(DT):
                v.scalar_tensor_tensor(hT[:, d, :], xT[:, d, :], v_out[:, d:d + 1], rstd[:], ALU.mult,
                                       ALU.mult).then_inc(on("y_ready"), 1)
            for t in range(3):
                n = TILES[t][1]
                dve.wait_ge(on("y_turned"), 2 * t + 2)
                v.tensor_copy(y_rows[0:n, t, 512:1024], bank[2 * t + 1][0:n, :]).then_inc(on("y_copied_v"), 1)

        @block.tensor
        def _(pe):
            t_ = nc.tensor
            next_unit = [0]

            def claim(label):
                b, n = plan[label]
                if n > 1:
                    pe.wait_ge(emptied[b], n - 1)
                return bank[b]

            def fill(label, ins):
                ins.then_inc(filled[plan[label][0]], 1)

            def unit():
                n = next_unit[0]
                next_unit[0] += 1
                pe.wait_ge(ring_loaded[n % RING], 16 * (n // RING + 1))
                src, kn, cols = units[n]
                return ring[:, n % RING, 0:kn * cols].rearrange("p (k n) -> p k n", k=kn)

            def frees(ins):
                if next_unit[0] > 1:
                    ins.then_inc(ring_used, 1)

            def turn(out, in_, rows):
                return t_.transpose(out, in_, ident[0:rows, 0:rows])

            pe.wait_ge(on("consts_ready"), 1)
            pe.wait_ge(on("c_loaded"), 2 * 16)
            b = claim("cond")
            for d in range(DT):
                ins = turn(b[:, d * NC:(d + 1) * NC], c_rows[0:NC, d * P:(d + 1) * P], NC)
            fill("cond", ins)
            pe.wait_ge(on("vec_loaded"), 10 * 16)
            b = claim("params")
            turn(b[:, 0:96], bada_rows[0:96, :], 96)
            turn(b[:, 96:156], vec_rows[0:60, :], 60)
            turn(b[:, 156:280], conv_b_rows[0:KB * CT, :], KB * CT)
            fill("params", turn(b[:, 280:292], conv_a_rows[0:KA * CT, :], KA * CT))
            pe.wait_ge(on("x_loaded"), 2 * 16)
            for d in range(DT):
                b = claim(f"x{d}")
                for t, (c0, n) in enumerate(TILES):
                    ins = turn(b[:, c0:c0 + n], x_rows[0:n, t, d * P:(d + 1) * P], n)
                fill(f"x{d}", ins)
            pe.wait_ge(on("states_loaded"), 2 * 16)
            for j in range(2):
                b = claim(f"state_b{j}")
                for t in range(2):
                    for h in range(2):
                        ins = turn(b[:, t * 240 + h * 120:t * 240 + (h + 1) * 120],
                                   state_b_rows[0:120, h, (2 * j + t) * P:(2 * j + t + 1) * P], 120)
                fill(f"state_b{j}", ins)
            b = claim("state_a")
            for t in range(CT):
                ins = turn(b[:, t * 16:(t + 1) * 16], state_a_rows[0:16, t * P:(t + 1) * P], 16)
            fill("state_a", ins)

            def column_sums(label, src, tiles):
                b = claim(label)
                for d in range(tiles):
                    ins = t_.matmul(b[:, 0:NT], ones[:], src[:, d, :], start=(d == 0), stop=(d == tiles - 1))
                fill(label, ins)

            def norm(n):
                pe.wait_ge(on("sq_ready"), n + 1)
                column_sums(f"ssq{n}", sq, DT)

            waiting = []

            def ada_turn():
                layer, blk = waiting.pop()
                bk, n = plan[f"acc{layer}_{blk}"]
                pe.wait_ge(emptied[bk], n)
                half = blk // HALF_BLOCKS
                if blk % HALF_BLOCKS == 0:
                    if layer or half:
                        pe.wait_ge(on("ada_taken"), 2 * layer + half)
                    else:
                        pe.wait_ge(emptied[6], plan["x4"][1])
                for f in range(4):
                    c = ((blk % HALF_BLOCKS) * 4 + f) * NC
                    ins = t_.matmul(bank[6][:, c:c + NC], ada_part[:, f * P:(f + 1) * P], pick_sum[:],
                                    start=(blk % HALF_BLOCKS == 0 and f == 0), stop=True, skip_group_check=True)
                ins.then_inc(on("ada_turned"), 1)

            def ada(layer, blk):
                if waiting:
                    ada_turn()
                label = f"acc{layer}_{blk}"
                b = claim(label)
                for h in range(KH):
                    w = unit()
                    for k in range(4):
                        ins = t_.matmul(b[32 * k:32 * k + 32, :], csT[:, h * 4 + k, :], w[:, k, :],
                                        start=(h == 0), stop=(h == KH - 1), skip_group_check=True)
                        if k == 0:
                            frees(ins)
                fill(label, ins)
                waiting.append((layer, blk))
                if (blk + 1) % HALF_BLOCKS == 0:
                    ada_turn()

            def gemm(labels, src, k_tiles, ready=None):
                banks = [None] * len(labels)
                for k0 in range(0, k_tiles, 4):
                    if ready:
                        ready(k0)
                    w = unit()
                    kn = min(4, k_tiles - k0)
                    for f, label in enumerate(labels):
                        if k0 == 0:
                            banks[f] = claim(label)
                        for k in range(kn):
                            ins = t_.matmul(banks[f][:, 0:NT], w[:, k, f * P:(f + 1) * P], src[:, k0 + k, :],
                                            start=(k0 + k == 0), stop=(k0 + k == k_tiles - 1))
                            if f == 0 and k == 0:
                                frees(ins)
                        if k0 + kn == k_tiles:
                            fill(labels[f], ins)

            def h_ready(n):
                def ready(k0):
                    if k0 == 0:
                        pe.wait_ge(on("hs_ready"), n + 1)
                    pe.wait_ge(on("h_ready"), n * DT + k0 + 4)
                return ready

            norm(0)
            act_ready = plan["cond"]
            pe.wait_ge(emptied[act_ready[0]], act_ready[1])
            def mixed_ready(k0):
                if k0 == 0:
                    pe.wait_ge(on("ya_ready"), 1)
                else:
                    pe.wait_ge(on("yb_ready"), CT)

            def hid0_ready(k0):
                for t in range(k0, min(k0 + 4, FT)):
                    bk, n = plan[f"up{t}"]
                    pe.wait_ge(emptied[bk], n)

            def mid():
                pe.wait_ge(on("conv_b_done"), 1)
                column_sums("ln_sum", yb, CT)
                pe.wait_ge(on("ln_sq_ready"), 1)
                column_sums("ln_ssq", gate_b, CT)
                pe.wait_ge(on("up_a_ready"), 1)
                pe.wait_ge(on("up_b_ready"), 1)
                for label, src in (("new_a_prompt", up_a[:, :, NP:]), ("new_a_sample", st_a[:, :, :, KA - 1]),
                                   ("new_b_prompt", up_b[:, :, NP:]), ("new_b_sample", st_b[:, :, :, KB - 1])):
                    b = claim(label)
                    n = src.shape[2]
                    for t in range(CT):
                        ins = t_.transpose(b[0:n, t * P:(t + 1) * P], src[:, t, :], ident[:])
                    fill(label, ins)

            for step in schedule():
                kind = step[0]
                if kind == "ada":
                    ada(*step[1:])
                elif kind == "in":
                    gemm([f"in{step[1]}_{t}" for t in range(4)], hT, DT, h_ready(0) if step[1] == IN_ORDER[0] else None)
                elif kind == "mid":
                    mid()
                elif kind == "out":
                    gemm([f"out{4 * step[1] + f}" for f in range(4)], mixed, DT, None if step[1] else mixed_ready)
                elif kind == "norm1":
                    norm(1)
                elif kind in ("gate", "up"):
                    gemm([f"{kind}{t}" for t in ffn_tiles(step[1])], hT, DT,
                         h_ready(1) if (kind, step[1]) == ("gate", 0) else None)
                elif kind == "state_c":
                    pe.wait_ge(on("state_c_loaded"), 16)
                    for j in range(2):
                        b = claim(f"state_c{j}")
                        for t in range(4):
                            ins = turn(b[:, t * 120:(t + 1) * 120],
                                       state_c_rows[0:120, (4 * j + t) * P:(4 * j + t + 1) * P], 120)
                        fill(f"state_c{j}", ins)
                elif kind == "down":
                    gemm([f"down{4 * step[1] + f}" for f in range(4)], hid0, FT, None if step[1] else hid0_ready)
            pe.wait_ge(on("ada_taken"), 4)
            norm(2)
            w = unit()
            for d in range(DT):
                g = d // 2
                if d % 2 == 0:
                    pe.wait_ge(on("diff_ready"), g + 1)
                b = claim(f"pool{d}")
                for k in range(2):
                    ins = t_.matmul(b[:, 0:NT], w[:, 2 * g + k, (d % 2) * P:(d % 2 + 1) * P], diff[:, 2 * g + k, :],
                                    start=(k == 0), stop=(k == 1))
                    if d == 0 and k == 0:
                        frees(ins)
                fill(f"pool{d}", ins)
            for what, c0, n in (("prompt", NP - CTX, CTX), ("sample", NP, NS)):
                for j in range(2):
                    label = f"new_c_{what}{j}"
                    b = claim(label)
                    for t in range(4):
                        ins = t_.transpose(b[0:n, t * P:(t + 1) * P], hT[:, 4 * j + t, c0:c0 + n], ident[:])
                    fill(label, ins)
            norm(3)
            pe.wait_ge(on("hs_ready"), 4)
            pe.wait_ge(on("h_ready"), 4 * DT)
            pe.wait_ge(on("router_loaded"), 2 * 16)
            b = claim("logits")
            for t, (c0, n) in enumerate(TILES):
                for k in range(DT):
                    ins = t_.matmul(b[0:n, t * NE:(t + 1) * NE], hT[:, k, c0:c0 + n], router[:, k, :],
                                    start=(t == 0 and k == 0), stop=(k == DT - 1), skip_group_check=True)
            fill("logits", ins)
            for t, (c0, n) in enumerate(TILES):
                for h in range(2):
                    label = f"rows{t}{h}"
                    b = claim(label)
                    for k in range(4):
                        ins = t_.transpose(b[0:n, k * P:(k + 1) * P], hT[:, 4 * h + k, c0:c0 + n], ident[:])
                    fill(label, ins)
            pe.wait_ge(on("mask_ready"), 1)
            b = claim("positions")
            first = True
            for t in range(3):
                for r in range(t + 1):
                    t_.matmul(b[:, t * NE:(t + 1) * NE], before[:] if r == t else ones[:], mask[:, r, :],
                              start=first, stop=(r == t), skip_group_check=True)
                    first = False
            for r in range(3):
                ins = t_.matmul(b[:, 3 * NE:4 * NE], ones[:], mask[:, r, :], start=False, stop=(r == 2),
                                skip_group_check=True)
            fill("positions", ins)
            pe.wait_ge(on("pm_ready"), 1)
            b = claim("turned")
            for t, (c0, n) in enumerate(TILES):
                ins = turn(b[0:2 * NE, c0:c0 + n], pm[0:n, t, :], n)
            fill("turned", ins)
            pe.wait_ge(on("pmT_ready"), 1)
            for kind, r0 in (("pos", 0), ("wgt", NE)):
                for e in range(NE):
                    label = f"{kind}{e}"
                    b = claim(label)
                    fill(label, t_.matmul(b[:, 0:NT], ident[0:2 * NE, r0 + e:r0 + e + 1].to_broadcast([2 * NE, P]),
                                          pmT[:], start=True, stop=True))

            def gather(q, w):
                pe.wait_ge(on("pick_ready"), q + 1)
                for b in range(4):
                    for i in range(2):
                        d = 2 * b + i
                        for t, (_, n) in enumerate(TILES):
                            ins = t_.matmul(bank[b][:, i * w:(i + 1) * w], h_rows[0:n, t, d * P:(d + 1) * P],
                                            pick[0:n, t, 0:w], start=(i == 0 and t == 0), stop=(t == 2),
                                            skip_group_check=True)
                    ins.then_inc(on("gathered"), 1)

            pe.wait_ge(on("rows_even"), 1)
            for bk in range(8):
                pe.wait_ge(emptied[bk], bank_total[bk])
            pe.wait_ge(on("flags_ready"), 1)
            passes = pe.value_load(flag[0:1, 2 * NE + 1:2 * NE + 2], min_val=1, max_val=2)
            wide = pe.value_load(flag[0:1, 0:1], min_val=0, max_val=1)
            with pe.If(wide == 1):
                gather(0, WIDE)
            with pe.Else():
                gather(0, NARROW)

            def expert_tensor(q, w):
                cur = {}
                n = [0]

                def load(key, k):
                    m = UNITS0 + n[0]
                    n[0] += 1
                    cur[key] = (m, ring[:, m % RING, :].rearrange("p (k n) -> p k n", k=k))

                def loaded(key):
                    m = cur[key][0]
                    pe.wait_ge(ring_loaded[m % RING],
                               q * (16 * EXPERT_UNITS // RING) + 16 * (m // RING + 1))

                def down(p):
                    pe.wait_ge(on("hid_ready"), q * PAIRS + (p + 1))
                    if p == 0:
                        pe.wait_ge(on("x_updated"), q * DT + DT)
                    loaded(("down", p))
                    wd = cur[("down", p)][1]
                    for j in range(2):
                        for d in range(DT):
                            ins = t_.matmul(bank[4 + d // 3][:, (d % 3) * w:(d % 3 + 1) * w], wd[:, j, d * P:(d + 1) * P],
                                            hid[p % 2][:, j * w:(j + 1) * w],
                                            start=(p == 0 and j == 0 and d % 3 == 0), stop=(p == PAIRS - 1 and j == 1),
                                            skip_group_check=True)
                            if j == 0 and d == 0 and (p % 2 == 0 or p == PAIRS - 1):
                                ins.then_inc(ring_used, 1 if p == PAIRS - 1 else 5 if p else 4)
                    return ins

                for p in range(PAIRS):
                    c = p // 2
                    if p % 2 == 0:
                        for key in ("gate", "up"):
                            for h in range(KH):
                                load((key, c, h), 4)
                        if c:
                            load(("down", p - 1), 2)
                        load(("down", p), 2)
                    for key, bk in (("gate", 2 * (p % 2)), ("up", 2 * (p % 2) + 1)):
                        if p == 0 and key == "gate":
                            pe.wait_ge(on("xg_ready"), q * 4 + 4)
                        if p >= 2:
                            pe.wait_ge(on("silu_ready" if key == "gate" else "hid_ready"), q * PAIRS + (p - 1))
                        if p % 2 == 0:
                            loaded((key, c, 0))
                            loaded((key, c, 1))
                        for i in range(2):
                            f = 2 * (p % 2) + i
                            for k in range(DT):
                                ins = t_.matmul(bank[bk][:, i * w:(i + 1) * w],
                                                cur[(key, c, k // 4)][1][:, k % 4, f * P:(f + 1) * P], xg[:, k, 0:w],
                                                start=(i == 0 and k == 0), stop=(k == DT - 1), skip_group_check=True)
                                if p % 2 == 0 and key == "gate" and i == 0 and k == 0:
                                    ins.then_inc(ring_used, 1)
                        ins.then_inc(on(f"{key}_done"), 1)
                    if p:
                        down(p - 1)
                load(("down", PAIRS - 1), 2)
                down(PAIRS - 1).then_inc(on("out_done"), 1)

            def combine(q, w):
                m = min(w, P)
                pe.wait_ge(on("outT_ready"), q + 1)
                for d in range(DT):
                    ins = t_.transpose(bank[7 if d < 4 else 4][0:m, (d % 4) * P:(d % 4 + 1) * P], outT[:, d, 0:m], ident[:])
                if w > P:
                    for d in range(DT):
                        ins = t_.transpose(bank[5 + d // 4][0:w - P, (d % 4) * P:(d % 4 + 1) * P], outT[:, d, P:w], ident[:])
                ins.then_inc(on("turned_out"), 1)
                pe.wait_ge(on("place_ready"), 2 * q + 2)
                pe.wait_ge(on("out_rows_ready"), q + 1)
                for d in range(DT):
                    if d >= 4:
                        pe.wait_ge(on("x_updated"), q * DT + (DT + d - 3))
                    b = bank[(7, 4, 5, 6)[d % 4]]
                    ins = t_.matmul(b[:, 0:NT], out_rows[0:m, d * P:(d + 1) * P], place[0:m, :], start=True, stop=(w <= P))
                    if w > P:
                        ins = t_.matmul(b[:, 0:NT], out_rows_b[0:w - P, d * P:(d + 1) * P], place_b[0:w - P, :],
                                        start=False, stop=True)
                    ins.then_inc(on("scattered"), 1)

            with pe.Fori(0, passes) as ps:
                with pe.Fori(0, NE) as e:
                    q = ps * NE + e
                    wide = pe.value_load(flag[0:1, bass.ds(q, 1)], min_val=0, max_val=1)
                    with pe.If(wide == 1):
                        expert_tensor(q, WIDE)
                    with pe.Else():
                        expert_tensor(q, NARROW)
                    wide_next = pe.value_load(flag[0:1, bass.ds(q + 1, 1)], min_val=0, max_val=1)
                    with pe.If(wide_next == 1):
                        gather(q + 1, WIDE)
                    with pe.Else():
                        gather(q + 1, NARROW)
                    with pe.If(wide == 1):
                        combine(q, WIDE)
                    with pe.Else():
                        combine(q, NARROW)

            pe.wait_ge(on("sq_ready"), 5)
            for d in range(DT):
                ins = t_.matmul(bank[0][:, 0:NT], ones[:], sq[:, d, :], start=(d == 0), stop=(d == DT - 1))
            ins.then_inc(on("ssq_final"), 1)
            pe.wait_ge(on("y_ready"), DT)
            for t, (c0, n) in enumerate(TILES):
                for h in range(2):
                    for k in range(4):
                        ins = t_.transpose(bank[2 * t + h][0:n, k * P:(k + 1) * P], hT[:, 4 * h + k, c0:c0 + n], ident[:])
                    ins.then_inc(on("y_turned"), 1)


_INS = ['x_prompt', 'x_sample', 'state_a', 'state_b', 'state_c', 'c_prompt', 'c_sample', 'w_ada', 'b_ada', 'norm_mix',
        'norm_ffn', 'norm_out', 'w_in', 'w_conv_a', 'w_conv_b', 'b_conv_b', 'ln_b_g', 'ln_b_b', 'w_out', 'w_ffn_gate',
        'w_ffn_up', 'w_ffn_down', 'w_pool', 'pool_scale', 'w_router', 'b_router', 'w_exp_gate', 'w_exp_up',
        'w_exp_down']
_OUTS = [(1, 256, 1024), (8, 1, 1024), (1, 1, 2, 512), (1, 8, 2, 512), (1, 1, 30, 512), (1, 8, 30, 512),
         (1, 1, 15, 1024), (1, 8, 15, 1024)]


def kernel(**inputs):
    import numpy as _np
    import concourse.bacc as _bacc
    from concourse import mybir as _mybir
    from concourse.bass_utils import run_bass_kernel_spmd as _run

    nc = _bacc.Bacc("TRN2", target_bir_lowering=False, num_devices=1)
    arrays, args = {}, []
    for name in _INS:
        a = _np.ascontiguousarray(inputs[name])
        arrays[f"in_{name}_dram"] = a
        args.append(nc.dram_tensor(f"in_{name}_dram", a.shape, _mybir.dt.from_np(a.dtype), kind="ExternalInput").ap())
    for i, shape in enumerate(_OUTS):
        args.append(nc.dram_tensor(f"out_{i}_dram", shape, _mybir.dt.float32, kind="ExternalOutput").ap())
    build(nc, *args)
    r = _run(nc, [arrays], core_ids=[0])
    return tuple(r.results[0][f"out_{i}_dram"] for i in range(len(_OUTS)))
```
